# Optimizing a Trainium2 kernel written in Bass

```python
import jax
import jax.numpy as jnp
from jax import lax
import numpy as np

D_MODEL = 1024
BATCH = 1
SEQ = 512
DEPTH = 1

HEAD_DIM = 64
HEADS_PER_MIXER = 4
N_MIXERS = 4
N_HEADS = N_MIXERS * HEADS_PER_MIXER
MIX_WIDTH = HEADS_PER_MIXER * HEAD_DIM
Q_BLOCK = 128
IDX_HEADS = 8
IDX_DIM = 64
TOPK_KEYS_MAX = 256
DILATED_PAIRS = ((128, 1), (512, 4), (2048, 16))
MOBA_BLOCK = 256
MOBA_TOPK = 3
MOBA_QBLOCK = 64
N_EXPERTS = 16
N_GROUPS = 4
TOPK_GROUPS = 1
TOPK_EXPERTS = 2
D_EXPERT = 512
N_ADA = 6
DN_ALPHA = (2 * DEPTH) ** 0.25
DN_BETA = (8 * DEPTH) ** -0.25
LN_EPS = 1e-5
IN_SPLITS = (N_HEADS * HEAD_DIM, N_HEADS * HEAD_DIM, N_HEADS * HEAD_DIM,
             IDX_HEADS * IDX_DIM, IDX_DIM, IDX_HEADS, HEADS_PER_MIXER)
IN_COLS = sum(IN_SPLITS)

kernel_name = 'hybrid_gated_sparse_mixers_moe'

def _layer_norm(x, g, b):
    xf = x.astype(jnp.float32)
    mu = jnp.mean(xf, axis=-1, keepdims=True)
    var = jnp.mean(jnp.square(xf - mu), axis=-1, keepdims=True)
    y = (xf - mu) * lax.rsqrt(var + LN_EPS) * g.astype(jnp.float32) + b.astype(jnp.float32)
    return y.astype(x.dtype)

def _alibi_slopes():
    n = 3 * HEADS_PER_MIXER
    s = 2.0 ** (-8.0 * np.arange(1, n + 1) / n)
    return jnp.asarray(s.reshape(HEADS_PER_MIXER, 3).T, dtype=jnp.float32)

def _masked_softmax(logits, mask):
    return jax.nn.softmax(jnp.where(mask, logits, -jnp.inf), axis=-1)

def _sweep_query_blocks(fn, block, *arrays):
    S = arrays[0].shape[1]
    nblk = S // block
    blocks = tuple(jnp.swapaxes(a.reshape(a.shape[0], nblk, block, *a.shape[2:]), 0, 1) for a in arrays)
    starts = jnp.arange(nblk, dtype=jnp.int32) * block
    out = lax.map(lambda xs: fn(xs[0], *xs[1]), (starts, blocks))
    out = jnp.swapaxes(out, 0, 1)
    return out.reshape(out.shape[0], S, *out.shape[3:])

def _dsa_attention(q, k, v, qi, ki, wi, slopes):
    B, S, H, Dh = q.shape
    k_top = min(TOPK_KEYS_MAX, S // 4)
    key_pos = jnp.arange(S, dtype=jnp.int32)
    b_idx = jnp.arange(B)[:, None, None]
    wi = wi.astype(jnp.float32) * (IDX_HEADS ** -0.5)
    scale = Dh ** -0.5

    def block(t0, qb, qib, wib):
        t = t0 + jnp.arange(Q_BLOCK, dtype=jnp.int32)
        rel = jax.nn.relu(jnp.einsum('bthd,bsd->bths', qib, ki).astype(jnp.float32))
        score = jnp.einsum('bths,bth->bts', rel, wib) * (IDX_DIM ** -0.5)
        score = jnp.where(key_pos[None, None, :] <= t[None, :, None], score, -jnp.inf)
        _, sel = lax.top_k(score, k_top)
        valid = sel <= t[None, :, None]
        kg = k[b_idx, sel]
        vg = v[b_idx, sel]
        logits = jnp.einsum('bthd,btkhd->bthk', qb, kg).astype(jnp.float32) * scale
        dist = (t[None, :, None] - sel).astype(jnp.float32)
        logits = logits - slopes[None, None, :, None] * dist[:, :, None, :]
        p = _masked_softmax(logits, valid[:, :, None, :])
        return jnp.einsum('bthk,btkhd->bthd', p.astype(v.dtype), vg)

    return _sweep_query_blocks(block, Q_BLOCK, q, qi, wi)

def _dilated_attention(q, k, v, slopes):
    B, S, H, Dh = q.shape
    scale = Dh ** -0.5

    def block(t0, qb):
        t = t0 + jnp.arange(Q_BLOCK, dtype=jnp.int32)
        outs, lses = [], []
        for window, dil in DILATED_PAIRS:
            offs = jnp.arange(window // dil + 1, dtype=jnp.int32) * dil
            pos = t[:, None] - offs[None, :]
            idx = jnp.maximum(pos, 0)
            kg = k[:, idx]
            vg = v[:, idx]
            logits = jnp.einsum('bthd,btnhd->bthn', qb, kg).astype(jnp.float32) * scale
            logits = logits - slopes[:, None] * offs.astype(jnp.float32)[None, :]
            logits = jnp.where((pos >= 0)[None, :, None, :], logits, -jnp.inf)
            lse = jax.nn.logsumexp(logits, axis=-1)
            p = jnp.exp(logits - lse[..., None])
            outs.append(jnp.einsum('bthn,btnhd->bthd', p.astype(v.dtype), vg))
            lses.append(lse)
        w = jax.nn.softmax(jnp.stack(lses, axis=0), axis=0)
        return jnp.sum(w[..., None].astype(v.dtype) * jnp.stack(outs, axis=0), axis=0)

    return _sweep_query_blocks(block, Q_BLOCK, q)

def _moba_attention(q, k, v, slopes):
    B, S, H, Dh = q.shape
    n_kb = -(-S // MOBA_BLOCK)
    pad = n_kb * MOBA_BLOCK - S
    kp = jnp.pad(k, ((0, 0), (0, pad), (0, 0), (0, 0)))
    vp = jnp.pad(v, ((0, 0), (0, pad), (0, 0), (0, 0)))
    kbh = kp.reshape(B, n_kb, MOBA_BLOCK, H, Dh).transpose(0, 3, 1, 2, 4)
    vbh = vp.reshape(B, n_kb, MOBA_BLOCK, H, Dh).transpose(0, 3, 1, 2, 4)
    k_mean = jnp.mean(kbh.astype(jnp.float32), axis=3)
    k_top = min(MOBA_TOPK, n_kb)
    n_sel = k_top * MOBA_BLOCK
    blk_ids = jnp.arange(n_kb, dtype=jnp.int32)
    in_blk = jnp.arange(MOBA_BLOCK, dtype=jnp.int32)
    b_idx = jnp.arange(B)[:, None, None, None]
    h_idx = jnp.arange(H)[None, None, :, None]
    scale = Dh ** -0.5

    def block(t0, qb):
        t = t0 + jnp.arange(MOBA_QBLOCK, dtype=jnp.int32)
        own = t0 // MOBA_BLOCK
        gate = jnp.einsum('bthd,bhnd->bthn', qb.astype(jnp.float32), k_mean)
        gate = jnp.where(blk_ids < own, gate, -jnp.inf)
        _, sel = lax.top_k(gate, k_top)
        sel_valid = sel < own
        kg = kbh[b_idx, h_idx, sel]
        vg = vbh[b_idx, h_idx, sel]
        lg_sel = jnp.einsum('bthd,bthkjd->bthkj', qb, kg).astype(jnp.float32) * scale
        dist_sel = (t[None, :, None, None, None] - (sel[..., None] * MOBA_BLOCK + in_blk)).astype(jnp.float32)
        lg_sel = lg_sel - slopes[None, None, :, None, None] * dist_sel
        lg_sel = jnp.where(sel_valid[..., None], lg_sel, -jnp.inf).reshape(B, MOBA_QBLOCK, H, n_sel)
        start = own * MOBA_BLOCK
        k_own = lax.dynamic_slice_in_dim(kp, start, MOBA_BLOCK, axis=1)
        v_own = lax.dynamic_slice_in_dim(vp, start, MOBA_BLOCK, axis=1)
        dist_own = (t[:, None] - (start + in_blk)[None, :]).astype(jnp.float32)
        lg_own = jnp.einsum('bthd,bshd->bths', qb, k_own).astype(jnp.float32) * scale
        lg_own = lg_own - slopes[None, None, :, None] * dist_own[None, :, None, :]
        lg_own = jnp.where((dist_own >= 0)[None, :, None, :], lg_own, -jnp.inf)
        p = jax.nn.softmax(jnp.concatenate([lg_sel, lg_own], axis=-1), axis=-1).astype(v.dtype)
        o_sel = jnp.einsum('bthn,bthnd->bthd', p[..., :n_sel], vg.reshape(B, MOBA_QBLOCK, H, n_sel, Dh))
        o_own = jnp.einsum('bths,bshd->bthd', p[..., n_sel:], v_own)
        return o_sel + o_own

    return _sweep_query_blocks(block, MOBA_QBLOCK, q)

def _forgetting_attention(q, k, v, f_logit):
    B, S, H, Dh = q.shape
    cum = jnp.cumsum(jax.nn.log_sigmoid(f_logit.astype(jnp.float32)), axis=1)
    cum_keys = jnp.transpose(cum, (0, 2, 1))
    key_pos = jnp.arange(S, dtype=jnp.int32)
    scale = Dh ** -0.5

    def block(t0, qb, cum_q):
        t = t0 + jnp.arange(Q_BLOCK, dtype=jnp.int32)
        logits = jnp.einsum('bthd,bshd->bhts', qb, k).astype(jnp.float32) * scale
        logits = logits + jnp.transpose(cum_q, (0, 2, 1))[..., None] - cum_keys[:, :, None, :]
        p = _masked_softmax(logits, (key_pos[None, :] <= t[:, None])[None, None])
        return jnp.einsum('bhts,bshd->bthd', p.astype(v.dtype), v)

    return _sweep_query_blocks(block, Q_BLOCK, q, cum)

def _grouped_moe(h, w_router, b_router, w_gate, w_up, w_down):
    B, S, D = h.shape
    per_group = N_EXPERTS // N_GROUPS
    scores = jax.nn.sigmoid((h @ w_router).astype(jnp.float32))
    biased = scores + b_router.astype(jnp.float32)
    g = biased.reshape(B, S, N_GROUPS, per_group)
    group_score = jnp.sum(lax.top_k(g, 2)[0], axis=-1)
    _, top_g = lax.top_k(group_score, TOPK_GROUPS)
    group_mask = jnp.sum(jax.nn.one_hot(top_g, N_GROUPS), axis=-2)
    expert_mask = jnp.repeat(group_mask, per_group, axis=-1) > 0
    _, top_e = lax.top_k(jnp.where(expert_mask, biased, -jnp.inf), TOPK_EXPERTS)
    sel = jnp.take_along_axis(scores, top_e, axis=-1)
    weights = sel / jnp.sum(sel, axis=-1, keepdims=True)
    combine = jnp.sum(jax.nn.one_hot(top_e, N_EXPERTS) * weights[..., None], axis=-2).astype(h.dtype)
    out = None
    for e in range(N_EXPERTS):
        hid = jax.nn.silu(h @ w_gate[e]) * (h @ w_up[e])
        term = combine[..., e:e + 1] * (hid @ w_down[e])
        out = term if out is None else out + term
    return out

def setup_inputs(seed: int = 0) -> dict:
    key = jax.random.key(seed)
    ks = jax.random.split(key, 18)

    def nrm(k, shape, scale):
        return jax.random.normal(k, shape, jnp.float32) * scale

    return {
        'x': nrm(ks[0], (BATCH, SEQ, D_MODEL), 1.0),
        'c': nrm(ks[1], (BATCH, D_MODEL), 1.0),
        'w_in': nrm(ks[2], (DEPTH, D_MODEL, IN_COLS), D_MODEL ** -0.5),
        'b_forget': 2.0 + nrm(ks[3], (DEPTH, HEADS_PER_MIXER), 0.5),
        'w_branch': nrm(ks[4], (DEPTH, N_MIXERS, MIX_WIDTH, D_MODEL), MIX_WIDTH ** -0.5),
        'w_merge_gate': nrm(ks[5], (DEPTH, N_MIXERS, D_MODEL, D_MODEL), D_MODEL ** -0.5),
        'w_out': nrm(ks[6], (DEPTH, D_MODEL, D_MODEL), DN_BETA * D_MODEL ** -0.5),
        'w_ada': nrm(ks[7], (DEPTH, D_MODEL, N_ADA * D_MODEL), 0.5 * D_MODEL ** -0.5),
        'b_ada': nrm(ks[8], (DEPTH, N_ADA * D_MODEL), 0.02),
        'ln1_g': 1.0 + nrm(ks[9], (DEPTH, D_MODEL), 0.02),
        'ln1_b': nrm(ks[10], (DEPTH, D_MODEL), 0.02),
        'ln2_g': 1.0 + nrm(ks[11], (DEPTH, D_MODEL), 0.02),
        'ln2_b': nrm(ks[12], (DEPTH, D_MODEL), 0.02),
        'w_router': nrm(ks[13], (D_MODEL, N_EXPERTS), D_MODEL ** -0.5),
        'b_router': nrm(ks[14], (N_EXPERTS,), 0.01),
        'w_exp_gate': nrm(ks[15], (DEPTH, N_EXPERTS, D_MODEL, D_EXPERT), D_MODEL ** -0.5),
        'w_exp_up': nrm(ks[16], (DEPTH, N_EXPERTS, D_MODEL, D_EXPERT), D_MODEL ** -0.5),
        'w_exp_down': nrm(ks[17], (DEPTH, N_EXPERTS, D_EXPERT, D_MODEL), DN_BETA * D_EXPERT ** -0.5),
    }

def reference(x, c, w_in, b_forget, w_branch, w_merge_gate, w_out, w_ada, b_ada,
              ln1_g, ln1_b, ln2_g, ln2_b, w_router, b_router,
              w_exp_gate, w_exp_up, w_exp_down):
    B, S, _ = x.shape
    slopes = _alibi_slopes()
    split_at = [int(v) for v in np.cumsum(IN_SPLITS)[:-1]]

    def heads(a, m):
        return a[:, :, m * HEADS_PER_MIXER:(m + 1) * HEADS_PER_MIXER]

    for l in range(DEPTH):
        ada = (c @ w_ada[l] + b_ada[l])[:, None, :]
        sh1, sc1, g1, sh2, sc2, g2 = jnp.split(ada, N_ADA, axis=-1)

        h = x * (1.0 + sc1) + sh1
        proj = h @ w_in[l]
        q, k, v, qi, ki, wi, fl = jnp.split(proj, split_at, axis=-1)
        q = q.reshape(B, S, N_HEADS, HEAD_DIM)
        k = k.reshape(B, S, N_HEADS, HEAD_DIM)
        v = v.reshape(B, S, N_HEADS, HEAD_DIM)
        qi = qi.reshape(B, S, IDX_HEADS, IDX_DIM)
        o_a = _dsa_attention(heads(q, 0), heads(k, 0), heads(v, 0), qi, ki, wi, slopes[0])
        o_b = _dilated_attention(heads(q, 1), heads(k, 1), heads(v, 1), slopes[1])
        o_c = _moba_attention(heads(q, 2), heads(k, 2), heads(v, 2), slopes[2])
        o_d = _forgetting_attention(heads(q, 3), heads(k, 3), heads(v, 3), fl + b_forget[l])
        mixed = None
        for m, o in enumerate((o_a, o_b, o_c, o_d)):
            gate = jax.nn.sigmoid(h @ w_merge_gate[l, m])
            term = gate * (o.reshape(B, S, MIX_WIDTH) @ w_branch[l, m])
            mixed = term if mixed is None else mixed + term
        y = mixed @ w_out[l]
        x = _layer_norm(DN_ALPHA * x + g1 * y, ln1_g[l], ln1_b[l])

        h2 = x * (1.0 + sc2) + sh2
        y2 = _grouped_moe(h2, w_router, b_router, w_exp_gate[l], w_exp_up[l], w_exp_down[l])
        x = _layer_norm(DN_ALPHA * x + g2 * y2, ln2_g[l], ln2_b[l])
    return x


_drawn_inputs = setup_inputs


def setup_inputs(seed=0):
    import zlib

    import numpy as np

    out = dict(_drawn_inputs(seed))
    spreads = {}
    factors = {}
    for name, (base, spread) in spreads.items():
        noise = np.random.default_rng([zlib.crc32(name.encode()), seed]).standard_normal(out[name].shape)
        drawn = base * np.exp(spread * noise) if base else spread * noise
        out[name] = jnp.asarray(drawn.astype(out[name].dtype))
    for name, factor in factors.items():
        out[name] = (out[name] * factor).astype(out[name].dtype)
    return out
```

```python
from contextlib import ExitStack

import numpy as np

import concourse.bass as bass
from concourse import mybir

F32 = mybir.dt.float32
ALU = mybir.AluOpType
ACT = mybir.ActivationFunctionType
AX_X = mybir.AxisListType.X

P = 128
S, D = 512, 1024
ST, KC = S // P, D // P
DH, HPM, MIXERS = 64, 4, 4
MW = DH * HPM
IH = 8
TOPK = min(256, S // 4)
E, DE, GROUPS = 16, 512, 4
FC = DE // P
OFF_Q, OFF_K, OFF_V = 0, D, 2 * D
OFF_QI = 3 * D
OFF_KI = OFF_QI + IH * DH
OFF_WI = OFF_KI + DH
EPS = 1e-5
ALPHA = 2 ** 0.25
SCALE = DH ** -0.5
MASKED = -1e30
TAKEN = -3e38
STEPS = HPM * ST
OFF = [P * i * (i + 1) // 2 for i in range(ST + 1)]
PACK = OFF[ST]
PJ0 = 6
PJN = 24
PJ_END = PJ0 + MIXERS * PJN


def constants():
    t = np.arange(S)[:, None]
    s = np.arange(S)[None, :]
    d = t - s
    causal = np.where(d >= 0, 0.0, MASKED)
    times = ((d <= 128) * 1 + (d % 4 == 0) * (d <= 512) + (d % 16 == 0) * (d <= 2048)) * (d >= 0)
    dilated = np.where(times > 0, np.log(np.maximum(times, 1)) / SCALE, MASKED)

    def pack(table):
        return np.concatenate([table[P * i:P * i + P, :P * i + P] for i in range(ST)], axis=1)

    masks = np.stack([pack(dilated), pack(causal), pack(causal)]).astype(np.float32)
    n = 3 * HPM
    slopes = (2.0 ** (-8.0 * np.arange(1, n + 1) / n)).reshape(HPM, 3).T.astype(np.float32)
    rows = np.zeros((3, HPM, PACK), np.float32)
    for i in range(ST):
        keys = np.arange(P * i + P) - P * i
        rows[:, :, OFF[i]:OFF[i + 1]] = slopes[:, :, None] * keys / SCALE
    ranks = np.concatenate([np.arange(GROUPS, 0, -1), np.arange(E, 0, -1)]).astype(np.float32)[None, :]
    return {"eye": np.eye(P, dtype=np.float32), "masks": masks, "alibi": rows, "ranks": ranks}


def build(nc, a, out):
    w_in = a["w_in"][0].rearrange("(k p) n -> p k n", p=P)
    w_gate_m = a["w_merge_gate"][0]
    w_branch = a["w_branch"][0]
    w_ada = a["w_ada"][0].rearrange("(k p) n -> p k n", p=P)
    w_out = a["w_out"][0].rearrange("(k p) n -> p k n", p=P)
    x_dram = a["x"][0].rearrange("(t p) n -> p t n", p=P)
    out_dram = out[0].rearrange("(t p) n -> p t n", p=P)
    rows_dram = nc.dram_tensor("row_bias", [MIXERS, HPM, PACK], F32, kind="Internal").ap()

    with ExitStack() as ctx:
        def sb(name, shape):
            return ctx.enter_context(nc.sbuf_tensor(name, shape, F32))

        def sem(name):
            return ctx.enter_context(nc.semaphore(name))

        KB = 256
        arena = sb("arena", [P, 96 * KB])

        def part(start_kb, kb):
            return arena[:, start_kb * KB:(start_kb + kb) * KB]

        ring = part(0, 32).rearrange("p (s k n) -> p s k n", s=2, k=KC)
        w_br = part(32, 8).rearrange("p (k n) -> p k n", k=2)
        w_qkv = part(40, 24).rearrange("p (m k n) -> p m k n", m=3, k=KC)
        row_b = part(64, 10).rearrange("p (s n) -> p s n", s=2)
        bias_t = part(74, 10).rearrange("p (s n) -> p s n", s=2)
        score = part(84, 6).rearrange("p (t n) -> p t n", t=3)
        work = part(90, 2)
        exp_w = [part(48, 48), part(0, 48)]
        w_eg = [w[:, 0:16 * KB].rearrange("p (k n) -> p k n", k=KC) for w in exp_w]
        w_eu = [w[:, 16 * KB:32 * KB].rearrange("p (k n) -> p k n", k=KC) for w in exp_w]
        w_ed = [w[:, 32 * KB:48 * KB].rearrange("p (k n) -> p k n", k=FC) for w in exp_w]

        hT = sb("hT", [P, KC, S])
        tokens = sb("tokens", [P, ST, D])
        gates = tokens[:].rearrange("p t n -> p (t n)").rearrange("p (k n) -> p k n", k=KC)
        mixedT = sb("mixedT", [P, KC, S])
        w_qi = mixedT[:]
        acc = mixedT[:].rearrange("p k n -> p (k n)").rearrange("p (t n) -> p t n", t=ST)
        bc = sb("bc", [P, 6, D])
        bcf = bc[:].rearrange("p a n -> p (a n)")
        qT = bcf[:, 0:1024].rearrange("p (c n) -> p c n", c=2)
        kT = bcf[:, 1024:2048].rearrange("p (c n) -> p c n", c=2)
        v_t = bcf[:, 2048:3072].rearrange("p (c n) -> p c n", c=ST)
        oT = bcf[:, 3072:4096].rearrange("p (c n) -> p c n", c=2)
        qiT = bcf[:, 4096:6144].rearrange("p (c n) -> p c n", c=4)
        kiT = sb("kiT", [P, S])
        mask_t = sb("mask_t", [P, 3, PACK])
        hidT = mask_t[:].rearrange("p a n -> p (a n)")[:, 0:2048].rearrange("p (c n) -> p c n", c=FC)
        silu_t = mask_t[:].rearrange("p a n -> p (a n)")[:, 2048:3072].rearrange("p (c n) -> p c n", c=2)
        soft = sb("soft", [P, 8, 512])
        logit = soft[:, 0:2, :]
        prob = soft[:, 2:4, :]
        probT = soft[:, 4:6, :].rearrange("p s (c n) -> p s c n", c=ST)
        gated = soft[:, 6:8, :]
        w_ki = soft[:, 6:8, :].rearrange("p a n -> p (a n)").rearrange("p (k n) -> p k n", k=KC)
        eye = sb("eye", [P, P])
        stage = sb("stage", [56, P])
        cols = sb("cols", [P, 56])
        ada_c = sb("ada_c", [P, 4, KC])
        w_if = sb("w_if", [P, KC, 12])
        w_r = sb("w_r", [P, KC, E])
        wi_t = sb("wi_t", [P, ST, IH])
        b_f = sb("b_f", [4, 1])
        fgs = part(74, 6)[0:HPM].rearrange("p (a n) -> p a n", a=3)
        best8 = sb("best8", [P, 8])
        peak = sb("peak", [P, 2])
        npeak = sb("npeak", [P, 2])
        rsum = sb("rsum", [P, 2])
        rinv = sb("rinv", [P, 2])
        c_rep = part(92, 4).rearrange("p (k n) -> p k n", k=KC)
        stats = sb("stats", [P, ST, 2, 6])
        mv = sb("mv", [P, ST, 2])
        rstd = sb("rstd", [P, ST])
        minus_half = sb("minus_half", [P, 1])
        dve_waits = sb("dve_waits", [P, STEPS])
        pool_waits = sb("pool_waits", [P, HPM])
        rank = sb("rank", [P, 4 + E])
        b_rb = sb("b_rb", [P, E])
        r = {n: sb("r_" + n, [P, ST, E]) for n in ("score", "biased", "m", "v", "s1", "s2", "comb")}
        g4 = {n: sb("g_" + n, [P, ST * GROUPS]) for n in ("sum", "pair", "sel")}
        one = {n: sb("o_" + n, [P, ST]) for n in ("a", "b")}

        banks = [ctx.enter_context(nc.psum_tensor(f"bank{i}", [P, 512], F32)) for i in range(8)]
        pj, sc_ps, tr_ps, o_ps = banks[0:2], banks[2:4], banks[4:6], banks[6:8]

        small_in = sem("small_in")
        x_in = sem("x_in")
        masks_in = sem("masks_in")
        rows_out = sem("rows_out")
        ring_in = [sem("ring_in0"), sem("ring_in1")]
        qi_in = sem("qi_in")
        qkv_in = sem("qkv_in")
        row_in = [sem("row_in0"), sem("row_in1")]
        br_in = sem("br_in")
        post_in = sem("post_in")
        xres_in = sem("xres_in")
        cols_t = sem("cols_t")
        cols_r = sem("cols_r")
        crep_r = sem("crep_r")
        ada1_c = sem("ada1_c")
        ada1_r = sem("ada1_r")
        ada2_c = sem("ada2_c")
        ada2_r = sem("ada2_r")
        pj_full = sem("pj_full")
        pj_free = [sem("pj_free0"), sem("pj_free1")]
        xt_full = sem("xt_full")
        h_ready = sem("h_ready")
        fl_full = sem("fl_full")
        fg_step = sem("fg_step")
        fg_ln = sem("fg_ln")
        ix_full = sem("ix_full")
        ix_relu = sem("ix_relu")
        ix_acc = sem("ix_acc")
        ix_mask = sem("ix_mask")
        zero_r = sem("zero_r")
        mixed_zero = sem("mixed_zero")
        topk_step = sem("topk_step")
        topk_done = sem("topk_done")
        bias_r = sem("bias_r")
        qk_full = sem("qk_full")
        logits_r = sem("logits_r")
        npeak_r = sem("npeak_r")
        exp_r = sem("exp_r")
        rinv_r = sem("rinv_r")
        prob_r = sem("prob_r")
        trans_full = sem("trans_full")
        probT_r = sem("probT_r")
        pv_done = sem("pv_done")
        o_r = sem("o_r")
        gates_r = sem("gates_r")
        mixed_r = sem("mixed_r")
        res_step = sem("res_step")
        ln_step = sem("ln_step")
        var_r = sem("var_r")
        eps_r = sem("eps_r")
        half_r = sem("half_r")
        rstd_r = sem("rstd_r")
        norm_r = sem("norm_r")
        gain_r = sem("gain_r")
        x1_r = sem("x1_r")
        h2t_full = sem("h2t_full")
        h2_ready = sem("h2_ready")
        route_full = sem("route_full")
        sig_r = sem("sig_r")
        rt = sem("rt")
        exp_in = [sem("exp_in0"), sem("exp_in1")]
        up_full = sem("up_full")
        silu_r = sem("silu_r")
        hid_r = sem("hid_r")
        down_full = sem("down_full")
        acc_zero = sem("acc_zero")
        acc_r = sem("acc_r")
        fin_r = sem("fin_r")
        out_done = sem("out_done")

        block = ctx.enter_context(nc.Block())

        @block.sync
        def _(sp):
            def ring_load(slot, src):
                sp.dma_start(ring[:, slot], src).then_inc(ring_in[slot], 16)

            def ada_half(comp, half):
                return w_ada[:, :, comp * D + 512 * half:comp * D + 512 * half + 512]

            def qkv_load(m):
                for j, off in enumerate((OFF_Q, OFF_K, OFF_V)):
                    sp.dma_start(w_qkv[:, j], w_in[:, :, bass.ds(m * MW + off, MW)]).then_inc(qkv_in, 16)

            def gate_load(m, half):
                wg = w_gate_m[bass.ds(m, 1)].rearrange("o (k p) n -> p (o k) n", p=P)
                ring_load(half, wg[:, :, 512 * half:512 * half + 512])

            def row_load(n, j):
                sp.dma_start(row_b[:, j % 2], rows_dram[bass.ds(n, 1), j].partition_broadcast(P)
                             .rearrange("p o n -> p (o n)")).then_inc(row_in[j % 2], 16)

            def branch_load(m):
                sp.dma_start(w_br, w_branch[bass.ds(m, 1)].rearrange("o (k p) n -> p (o k) n", p=P)).then_inc(br_in, 16)

            sp.dma_start(stage[0:8, :], a["c"].rearrange("o (k p) -> (o k) p", p=P)).then_inc(small_in, 16)
            sp.dma_start(stage[8:56, :], a["b_ada"].rearrange("o (k p) -> (o k) p", p=P)).then_inc(small_in, 16)
            sp.dma_start(eye[:], a["eye"]).then_inc(small_in, 16)
            ring_load(0, ada_half(0, 0))
            ring_load(1, ada_half(0, 1))
            sp.dma_start(tokens[:], x_dram).then_inc(x_in, 16)
            sp.wait_ge(ada1_c, 1)
            ring_load(0, ada_half(1, 0))
            sp.wait_ge(ada1_c, 2)
            ring_load(1, ada_half(1, 1))
            sp.dma_start(w_if[:], w_in[:, :, OFF_WI:OFF_WI + 12]).then_inc(qi_in, 16)
            sp.dma_start(b_f[:], a["b_forget"].rearrange("o h -> h o")).then_inc(qi_in, 16)
            sp.dma_start(w_ki[:, :, 0:DH], w_in[:, :, OFF_KI:OFF_KI + DH]).then_inc(qi_in, 16)
            sp.dma_start(w_ki[:, :, DH:P], w_in[:, :, OFF_KI:OFF_KI + DH]).then_inc(qi_in, 16)
            sp.dma_start(w_qi, w_in[:, :, OFF_QI:OFF_QI + 512]).then_inc(qi_in, 16)
            qkv_load(1)
            sp.wait_ge(ada1_c, 3)
            gate_load(1, 0)
            sp.wait_ge(ada1_c, 4)
            gate_load(1, 1)
            branch_load(1)
            sp.dma_start(mask_t[:], a["masks"].rearrange("m p n -> p m n")).then_inc(masks_in, 16)
            sp.dma_start(rows_dram[0:2], a["alibi"][1:3]).then_inc(rows_out, 16)
            sp.dma_start(rows_dram[3], a["alibi"][0]).then_inc(rows_out, 16)
            sp.wait_ge(fg_step, 7)
            for i in range(ST):
                sp.dma_start(rows_dram[2, :, OFF[i]:OFF[i + 1]], fgs[:, 2, 0:P * i + P]).then_inc(rows_out, 16)
            sp.wait_ge(rows_out, 16 * (2 + ST))
            row_load(0, 0)
            row_load(0, 1)

            def rows_late(n):
                sp.wait_ge(bias_r, 4 * n + 1)
                row_load(n, 2)
                sp.wait_ge(bias_r, 4 * n + 2)
                row_load(n, 3)

            def next_loads(n, m):
                rows_late(n)
                sp.wait_ge(pj_full, PJN * n + PJ0 + 8)
                qkv_load(m)
                sp.wait_ge(pj_full, PJN * n + PJ0 + 12)
                gate_load(m, 0)
                sp.wait_ge(bias_r, 4 * n + 3)
                row_load(n + 1, 0)
                sp.wait_ge(bias_r, 4 * n + 4)
                row_load(n + 1, 1)
                sp.wait_ge(pj_full, PJN * n + PJ0 + 16)
                gate_load(m, 1)
                sp.wait_ge(pj_full, PJN * n + PJ0 + 24)
                branch_load(m)

            with sp.Fori(0, 2) as n:
                next_loads(n, n + 2)
            next_loads(2, 0)
            rows_late(3)
            sp.wait_ge(pj_full, PJN * 3 + PJ0 + 12)
            ring_load(0, ada_half(2, 0))
            sp.wait_ge(pj_full, PJN * 3 + PJ0 + 16)
            ring_load(1, ada_half(2, 1))
            sp.wait_ge(pj_full, PJ_END)
            for row, (name, off) in enumerate((("b_ada", 2 * D), ("b_ada", 5 * D), ("ln1_g", 0),
                                               ("ln1_b", 0), ("ln2_g", 0), ("ln2_b", 0))):
                sp.dma_start(bc[:, row], a[name][0, off:off + D].partition_broadcast(P)).then_inc(post_in, 16)
            sp.dma_start(w_r[:], a["w_router"].rearrange("(k p) n -> p k n", p=P)).then_inc(post_in, 16)
            sp.dma_start(b_rb[:], a["b_router"].partition_broadcast(P)).then_inc(post_in, 16)
            sp.dma_start(rank[:], a["ranks"][0].partition_broadcast(P)).then_inc(post_in, 16)
            sp.wait_ge(pj_free[0], PJ_END // 2)
            sp.wait_ge(pj_free[1], PJ_END // 2)
            sp.dma_start(tokens[:], x_dram).then_inc(xres_in, 16)
            for j in range(2):
                sp.wait_ge(pj_full, PJ_END + 1 + j)
                ring_load(j, ada_half(5, j))
            for j in range(2):
                sp.wait_ge(pj_full, PJ_END + 3 + j)
                ring_load(j, ada_half(3, j))
            for j in range(2):
                sp.wait_ge(ada2_c, 1 + j)
                ring_load(j, ada_half(4, j))
            for j in range(2):
                sp.wait_ge(ada2_c, 3 + j)
                ring_load(j, w_out[:, :, 512 * j:512 * j + 512])

            def expert_load(slot, e):
                for dst, name in ((w_eg, "w_exp_gate"), (w_eu, "w_exp_up"), (w_ed, "w_exp_down")):
                    src = a[name][0, bass.ds(e, 1)].rearrange("o (k p) n -> p (o k) n", p=P)
                    sp.dma_start(dst[slot], src).then_inc(exp_in[slot], 16)

            sp.wait_ge(logits_r, STEPS * MIXERS)
            expert_load(0, 0)
            sp.wait_ge(pj_full, PJ_END + 12)
            expert_load(1, 1)
            with sp.Fori(1, E // 2) as g:
                for slot in range(2):
                    sp.wait_ge(down_full, 16 * g - 8 + 8 * slot)
                    expert_load(slot, 2 * g + slot)
            for t in range(ST):
                sp.wait_ge(fin_r, t + 1)
                sp.dma_start(out_dram[:, t], tokens[:, t]).then_inc(out_done, 16)
            sp.wait_ge(out_done, 16 * ST)

        @block.tensor
        def _(pe):
            def take(use):
                if use >= 2:
                    pe.wait_ge(pj_free[use % 2], use // 2)
                return pj[use % 2]

            def columns(ps, slot, col0):
                for c in range(4):
                    for k in range(KC):
                        mm = pe.matmul(ps[:, col0 + c:col0 + c + 1], ring[:, slot, k, c * P:c * P + P],
                                       cols[:, k:k + 1], start=(k == 0), stop=(k == KC - 1))
                return mm

            pe.wait_ge(small_in, 48)
            pe.transpose(tr_ps[0][:, 0:56], stage[:], eye[0:56, 0:56]).then_inc(cols_t, 1)
            pe.wait_ge(cols_r, 1)
            for half in range(4):
                pe.wait_ge(ring_in[half % 2], 16 * (half // 2 + 1))
                columns(sc_ps[1], half % 2, 4 * half).then_inc(ada1_c, 1)
            pe.wait_ge(x_in, 16)
            for k in range(KC):
                if k >= 2:
                    pe.wait_ge(h_ready, k - 1)
                for t in range(ST):
                    mm = pe.transpose(tr_ps[k % 2][:, t * P:t * P + P], tokens[:, t, k * P:k * P + P], eye[:])
                mm.then_inc(xt_full, 1)
            pe.wait_ge(h_ready, KC)
            pe.wait_ge(qi_in, 80)
            for use in range(5):
                lhs = w_qi[:, :, use * P:use * P + P] if use < 4 else w_ki
                ps = take(use)
                for k in range(KC):
                    mm = pe.matmul(ps[:], lhs[:, k, :], hT[:, k, :], start=(k == 0), stop=(k == KC - 1))
                mm.then_inc(pj_full, 1)
            for k in range(KC):
                mm = pe.matmul(o_ps[0][0:HPM, :], w_if[:, k, IH:IH + HPM], hT[:, k, :],
                               start=(k == 0), stop=(k == KC - 1))
            mm.then_inc(fl_full, 1)
            ps = take(5)
            for t in range(ST):
                for k in range(KC):
                    mm = pe.matmul(ps[:, IH * t:IH * t + IH], hT[:, k, t * P:t * P + P], w_if[:, k, 0:IH],
                                   start=(k == 0), stop=(k == KC - 1))
            mm.then_inc(pj_full, 1)
            pe.wait_ge(pj_free[0], 3)
            pe.wait_ge(pj_free[1], 2)
            pe.wait_ge(ada1_r, 1)
            n = 0
            for i in range(1, ST):
                for h in range(IH):
                    if n >= 2:
                        pe.wait_ge(ix_relu, n - 1)
                    lo = DH * (h % 2)
                    pe.matmul(sc_ps[n % 2][:, 0:P * i + P], qiT[lo:lo + DH, h // 2, i * P:i * P + P],
                              kiT[lo:lo + DH, 0:P * i + P], start=True, stop=True).then_inc(ix_full, 1)
                    n += 1

            def mixer(n):
                half = PJ0 // 2 + PJN // 2 * n

                def bank(u):
                    pe.wait_ge(pj_free[u % 2], half + u // 2)
                    return pj[u % 2]

                pe.wait_ge(qkv_in, 48 * n + 48)
                for u in range(4):
                    ps = bank(u)
                    for k in range(KC):
                        mm = pe.matmul(ps[:], w_qkv[:, u // 2, k, (u % 2) * P:(u % 2) * P + P], hT[:, k, :],
                                       start=(k == 0), stop=(k == KC - 1))
                    mm.then_inc(pj_full, 1)
                for t in range(ST):
                    ps = bank(4 + t)
                    for k in range(KC):
                        mm = pe.matmul(ps[:, 0:MW], hT[:, k, t * P:t * P + P], w_qkv[:, 2, k, :],
                                       start=(k == 0), stop=(k == KC - 1))
                    mm.then_inc(pj_full, 1)

                def gate_half(s):
                    c = s // 2
                    if s % 8 == 0:
                        pe.wait_ge(ring_in[s // 8], 16 * n + 48)
                    ps = bank(8 + c) if s % 2 == 0 else pj[c % 2]
                    for k in range(4 * (s % 2), 4 * (s % 2) + 4):
                        mm = pe.matmul(ps[:], ring[:, c // 4, k, (c % 4) * P:(c % 4) * P + P], hT[:, k, :],
                                       start=(k == 0), stop=(k == KC - 1))
                    if s % 2:
                        mm.then_inc(pj_full, 1)

                def scores(s):
                    h, i = divmod(s, ST)
                    lo = DH * (h % 2)
                    if s < 2:
                        pe.wait_ge(ix_relu, IH * (ST - 1))
                    if s >= 2:
                        pe.wait_ge(logits_r, STEPS * n + s - 1)
                    pe.matmul(sc_ps[s % 2][:, 0:P * i + P], qT[lo:lo + DH, h // 2, i * P:i * P + P],
                              kT[lo:lo + DH, h // 2, 0:P * i + P], start=True, stop=True).then_inc(qk_full, 1)

                def turn(s):
                    pe.wait_ge(prob_r, STEPS * n + s + 1)
                    if s >= 2:
                        pe.wait_ge(probT_r, STEPS * n + s - 1)
                    for j in range(s % ST + 1):
                        mm = pe.transpose(tr_ps[s % 2][:, j * P:j * P + P], prob[:, s % 2, j * P:j * P + P], eye[:])
                    mm.then_inc(trans_full, 1)

                def values(s):
                    h, i = divmod(s, ST)
                    lo = DH * (h % 2)
                    pe.wait_ge(probT_r, STEPS * n + s + 1)
                    if s == 0:
                        pe.wait_ge(fg_step, 1)
                    for j in range(i + 1):
                        mm = pe.matmul(o_ps[h // 2][lo:lo + DH, i * P:i * P + P], v_t[:, j, h * DH:h * DH + DH],
                                       probT[:, s % 2, j, :], start=(j == 0), stop=(j == i))
                    mm.then_inc(pv_done, 1)

                pe.wait_ge(pj_free[0], half + 4)
                pe.wait_ge(pj_free[1], half + 4)
                for s in range(STEPS + 2):
                    if s < STEPS:
                        scores(s)
                        gate_half(s)
                    if 1 <= s <= STEPS:
                        turn(s - 1)
                    if s >= 2:
                        values(s - 2)
                pe.wait_ge(br_in, 16 * n + 16)
                pe.wait_ge(o_r, 2 * n + 2)
                for c in range(KC):
                    ps = bank(16 + c)
                    for k in range(2):
                        mm = pe.matmul(ps[:], w_br[:, k, c * P:c * P + P], oT[:, k, :], start=(k == 0), stop=(k == 1))
                    mm.then_inc(pj_full, 1)

            with pe.Fori(0, 3) as n:
                mixer(n)
            mixer(3)

            pe.wait_ge(crep_r, KC)
            for j in range(4):
                pe.wait_ge(ring_in[j % 2], 16 * (7 + j // 2))
                ps = take(PJ_END + j)
                for k in range(KC):
                    mm = pe.matmul(ps[:], c_rep[:, k, :], ring[:, j % 2, k, :], start=(k == 0), stop=(k == KC - 1))
                mm.then_inc(pj_full, 1)
            for j in range(4):
                pe.wait_ge(ring_in[j % 2], 16 * (9 + j // 2))
                columns(sc_ps[1], j % 2, 4 * j).then_inc(ada2_c, 1)
            pe.wait_ge(mixed_r, KC * MIXERS)
            for half in range(2):
                pe.wait_ge(ring_in[half], 16 * 11)
                for t in range(ST):
                    ps = take(PJ_END + 4 + 4 * half + t)
                    for k in range(KC):
                        mm = pe.matmul(ps[:], mixedT[:, k, t * P:t * P + P], ring[:, half, k, :],
                                       start=(k == 0), stop=(k == KC - 1))
                    mm.then_inc(pj_full, 1)
            pe.wait_ge(x1_r, ST)
            for k in range(KC):
                if k >= 2:
                    pe.wait_ge(h2_ready, k - 1)
                for t in range(ST):
                    mm = pe.transpose(tr_ps[k % 2][:, t * P:t * P + P], tokens[:, t, k * P:k * P + P], eye[:])
                mm.then_inc(h2t_full, 1)
            pe.wait_ge(h2_ready, KC)
            pe.wait_ge(post_in, 16 * 9)
            for t in range(ST):
                for k in range(KC):
                    mm = pe.matmul(sc_ps[0][:, E * t:E * t + E], hT[:, k, t * P:t * P + P], w_r[:, k, :],
                                   start=(k == 0), stop=(k == KC - 1))
            mm.then_inc(route_full, 1)
            pe.wait_ge(sig_r, 1)

            def expert(slot, e, turn, first=False):
                pe.wait_ge(exp_in[slot], 48 * turn + 48)
                for f in range(FC):
                    if f >= 2:
                        pe.wait_ge(hid_r, FC * e + f - 1)
                    for w, b in ((w_eg[slot], 0), (w_eu[slot], 1)):
                        for k in range(KC):
                            mm = pe.matmul(banks[2 * (f % 2) + b][:], w[:, k, f * P:f * P + P], hT[:, k, :],
                                           start=(k == 0), stop=(k == KC - 1))
                    mm.then_inc(up_full, 1)
                pe.wait_ge(hid_r, FC * e + FC)
                for n in range(2 * ST):
                    half, t = divmod(n, ST)
                    if n >= 4 or not first:
                        pe.wait_ge(acc_r, 8 * e + n - 3)
                    for f in range(FC):
                        mm = pe.matmul(banks[4 + n % 4][:], hidT[:, f, t * P:t * P + P],
                                       w_ed[slot][:, f, 512 * half:512 * half + 512],
                                       start=(f == 0), stop=(f == FC - 1))
                    mm.then_inc(down_full, 1)

            expert(0, 0, 0, first=True)
            expert(1, 1, 0)
            with pe.Fori(1, E // 2) as g:
                for slot in range(2):
                    expert(slot, 2 * g + slot, g)

        @block.scalar
        def _(act):
            act.wait_ge(ada1_r, 1)
            for k in range(KC):
                act.wait_ge(xt_full, k + 1)
                act.activation(hT[:, k, :], tr_ps[k % 2][:], ACT.Identity, bias=ada_c[:, 0, k:k + 1],
                               scale=ada_c[:, 1, k:k + 1]).then_inc(h_ready, 1)
            for use in range(5):
                act.wait_ge(pj_full, use + 1)
                act.activation(qiT[:, use, :] if use < 4 else kiT[:], pj[use % 2][:], ACT.Copy)\
                   .then_inc(pj_free[use % 2], 1)
            act.wait_ge(fg_step, 3)
            act.activation(fgs[:, 1, :], fgs[:, 1, :], ACT.Exp, scale=-1.0).then_inc(fg_ln, 1)
            act.wait_ge(fg_ln, 1)
            act.activation(fgs[:, 1, :], fgs[:, 1, :], ACT.Ln, bias=1.0).then_inc(fg_ln, 1)
            n = 0
            for i in range(1, ST):
                for h in range(IH):
                    act.wait_ge(ix_full, n + 1)
                    if n >= 2:
                        act.wait_ge(ix_acc, n - 1)
                    act.activation(logit[:, n % 2, 0:P * i + P], sc_ps[n % 2][:, 0:P * i + P], ACT.Relu)\
                       .then_inc(ix_relu, 1)
                    n += 1

            def mixer(n):
                base = PJ0 + PJN * n
                half = PJ0 // 2 + PJN // 2 * n
                for u in range(8):
                    act.wait_ge(pj_full, base + u + 1)
                    if u < 4:
                        dst, src = (qT, kT)[u // 2][:, u % 2, :], pj[u % 2][:]
                    else:
                        dst, src = v_t[:, u - 4, :], pj[u % 2][:, 0:MW]
                    act.activation(dst, src, ACT.Copy).then_inc(pj_free[u % 2], 1)
                for s in range(STEPS + 1):
                    b, w = s % 2, P * (s % ST) + P
                    if s < STEPS:
                        act.wait_ge(npeak_r, STEPS * n + s + 1)
                        if s >= 2:
                            act.wait_ge(trans_full, STEPS * n + s - 1)
                        act.activation(prob[:, b, 0:w], logit[:, b, 0:w], ACT.Exp, bias=npeak[:, b:b + 1],
                                       accum_out=rsum[:, b:b + 1]).then_inc(exp_r, 1)
                    if s >= 1:
                        b, w = (s - 1) % 2, P * ((s - 1) % ST) + P
                        act.wait_ge(rinv_r, STEPS * n + s)
                        act.activation(prob[:, b, 0:w], prob[:, b, 0:w], ACT.Copy, scale=rinv[:, b:b + 1])\
                           .then_inc(prob_r, 1)
                    if s % 2 == 0 and s:
                        c = s // 2 - 1
                        act.wait_ge(pj_full, base + 9 + c)
                        act.activation(gates[:, c, :], pj[c % 2][:], ACT.Copy).then_inc(pj_free[c % 2], 1)
                act.wait_ge(pj_free[0], half + 8)
                act.wait_ge(pj_free[1], half + 8)
                act.activation(gates[:, :, :], gates[:, :, :], ACT.Sigmoid).then_inc(gates_r, 1)

            with act.Fori(0, 3) as n:
                mixer(n)
            mixer(3)

            act.wait_ge(ada2_r, 1)
            for k in range(KC):
                act.wait_ge(h2t_full, k + 1)
                act.activation(hT[:, k, :], tr_ps[k % 2][:], ACT.Identity, bias=ada_c[:, 2, k:k + 1],
                               scale=ada_c[:, 3, k:k + 1]).then_inc(h2_ready, 1)
            act.wait_ge(route_full, 1)
            act.activation(r["score"][:].rearrange("p t e -> p (t e)"), sc_ps[0][:, 0:ST * E],
                           ACT.Sigmoid).then_inc(sig_r, 1)
            with act.Fori(0, E) as e:
                for f in range(FC):
                    act.wait_ge(up_full, FC * e + f + 1)
                    if f >= 2:
                        act.wait_ge(hid_r, FC * e + f - 1)
                    act.activation(silu_t[:, f % 2, :], banks[2 * (f % 2)][:], ACT.Silu).then_inc(silu_r, 1)

        @block.vector
        def _(dve):
            dve.wait_ge(cols_t, 1)
            dve.tensor_copy(cols[:], tr_ps[0][:, 0:56]).then_inc(cols_r, 1)
            dve.wait_ge(cols_r, 1)
            for k in range(KC):
                dve.tensor_scalar(c_rep[:, k, :], eye[:], 0.0, cols[:, k:k + 1], ALU.mult, ALU.add).then_inc(crep_r, 1)
            dve.wait_ge(ada1_c, 4)
            dve.tensor_tensor(ada_c[:, 0, :], sc_ps[1][:, 0:8], cols[:, 8:16], ALU.add)
            dve.scalar_tensor_tensor(out=ada_c[:, 1, :], in0=sc_ps[1][:, 8:16], scalar=1.0, in1=cols[:, 16:24],
                                     op0=ALU.add, op1=ALU.add).then_inc(ada1_r, 1)
            dve.wait_ge(fl_full, 1)
            dve.tensor_scalar(fgs[:, 0, :], o_ps[0][0:HPM, :], b_f[:], None, ALU.add).then_inc(fg_step, 1)
            dve.wait_ge(fg_step, 1)
            dve.scalar_tensor_tensor(out=fgs[:, 1, :], in0=fgs[:, 0, :], scalar=-1.0, in1=fgs[:, 0, :],
                                     op0=ALU.mult, op1=ALU.max).then_inc(fg_step, 1)
            dve.tensor_scalar(fgs[:, 2, :], fgs[:, 0, :], 0.0, None, ALU.min).then_inc(fg_step, 1)
            dve.wait_ge(pj_full, 6)
            dve.tensor_scalar(wi_t[:].rearrange("p t h -> p (t h)"), pj[1][:, 0:ST * IH], IH ** -0.5 * DH ** -0.5, None,
                              ALU.mult).then_inc(pj_free[1], 1)
            dve.memset(score, MASKED).then_inc(zero_r, 1)
            dve.wait_ge(fg_ln, 2)
            dve.wait_ge(fg_step, 3)
            dve.tensor_tensor(fgs[:, 1, :], fgs[:, 2, :], fgs[:, 1, :], ALU.subtract).then_inc(fg_step, 1)
            dve.wait_ge(fg_step, 4)
            dve.memset(fgs[:, 2, :], 1.0).then_inc(fg_step, 1)
            dve.wait_ge(fg_step, 5)
            dve.tensor_tensor_scan(fgs[:, 0, :], fgs[:, 2, :], fgs[:, 1, :], 0.0, ALU.mult, ALU.add).then_inc(fg_step, 1)
            dve.wait_ge(fg_step, 6)
            dve.tensor_scalar(fgs[:, 2, :], fgs[:, 0, :], -1.0 / SCALE, None, ALU.mult).then_inc(fg_step, 1)
            dve.wait_ge(zero_r, 1)
            dve.wait_ge(pj_free[1], 3)
            dve.wait_ge(masks_in, 16)
            n = 0
            for i in range(1, ST):
                w = P * i + P
                for h in range(IH):
                    dve.wait_ge(ix_relu, n + 1)
                    wi = wi_t[:, i, h:h + 1]
                    if h == 0:
                        dve.tensor_scalar(score[:, i - 1, 0:w], logit[:, n % 2, 0:w], wi, None, ALU.mult).then_inc(ix_acc, 1)
                    else:
                        dve.wait_ge(ix_acc, n)
                        dve.scalar_tensor_tensor(out=score[:, i - 1, 0:w], in0=logit[:, n % 2, 0:w], scalar=wi,
                                                 in1=score[:, i - 1, 0:w], op0=ALU.mult, op1=ALU.add).then_inc(ix_acc, 1)
                    n += 1
                dve.wait_ge(ix_acc, n)
                dve.tensor_tensor(score[:, i - 1, P * i:w], score[:, i - 1, P * i:w],
                                  mask_t[:, 1, OFF[i] + P * i:OFF[i + 1]], ALU.add).then_inc(ix_mask, 1)
            dve.wait_ge(ix_mask, ST - 1)

            def topk(n):
                dve.tensor_copy(work, score[:, bass.ds(n, 1), :].rearrange("p o n -> p (o n)")).then_inc(topk_step, 1)
                for i in range(TOPK // 8):
                    dve.wait_ge(topk_step, 2 * i + 1)
                    dve.max(best8[:], work).then_inc(topk_step, 1)
                    dve.wait_ge(topk_step, 2 * i + 2)
                    dve.match_replace(work, best8[:], work, TAKEN).then_inc(topk_step, 1)
                dve.wait_ge(topk_step, TOPK // 4 + 1)
                dve.tensor_scalar(score[:, bass.ds(n, 1), :].rearrange("p o n -> p (o n)"), work, TAKEN / 2, MASKED,
                                  ALU.is_gt, ALU.mult).then_inc(topk_done, 1)
                dve.sem_clear(topk_step)

            def mixer(n):
                base = PJ0 + PJN * n
                for s in range(STEPS + 2):
                    if s < STEPS:
                        h, i = divmod(s, ST)
                        b, w = s % 2, P * i + P
                        dve.wait_ge(qk_full, STEPS * n + s + 1)
                        if i == 0:
                            dve.wait_ge(bias_r, HPM * n + h + 1)
                        if s >= 2:
                            dve.wait_ge(exp_r, STEPS * n + s - 1)
                        dve.memset(dve_waits[:, s:s + 1], 0.0)
                        dve.tensor_tensor_reduce(logit[:, b, 0:w], sc_ps[b][:, 0:w], bias_t[:, h % 2, OFF[i]:OFF[i + 1]],
                                                 SCALE, TAKEN, ALU.add, ALU.max, peak[:, b:b + 1]).then_inc(logits_r, 1)
                        dve.wait_ge(logits_r, STEPS * n + s + 1)
                        dve.tensor_scalar(npeak[:, b:b + 1], peak[:, b:b + 1], -1.0, None, ALU.mult).then_inc(npeak_r, 1)
                    if 1 <= s <= STEPS:
                        b = (s - 1) % 2
                        dve.wait_ge(exp_r, STEPS * n + s)
                        dve.reciprocal(rinv[:, b:b + 1], rsum[:, b:b + 1]).then_inc(rinv_r, 1)
                    if s >= 2:
                        j = s - 2
                        b, w = j % 2, P * (j % ST) + P
                        dve.wait_ge(trans_full, STEPS * n + j + 1)
                        if j >= 2:
                            dve.wait_ge(pv_done, STEPS * n + j - 1)
                        dve.tensor_copy(probT[:, b].rearrange("p c n -> p (c n)")[:, 0:w], tr_ps[b][:, 0:w]).then_inc(probT_r, 1)
                    if s == 10:
                        dve.wait_ge(pv_done, STEPS * n + 8)
                        dve.tensor_copy(oT[:, 0, :], o_ps[0][:]).then_inc(o_r, 1)
                dve.wait_ge(pv_done, STEPS * n + 16)
                dve.tensor_copy(oT[:, 1, :], o_ps[1][:]).then_inc(o_r, 1)
                dve.wait_ge(gates_r, n + 1)
                for c in range(KC):
                    dve.wait_ge(pj_full, base + 17 + c)
                    if c >= 2:
                        dve.wait_ge(mixed_r, KC * n + c - 1)
                    dve.tensor_tensor(gated[:, c % 2, :], pj[c % 2][:], gates[:, c, :], ALU.mult).then_inc(pj_free[c % 2], 1)

            with dve.Fori(0, 3) as n:
                topk(n)
                mixer(n)
            mixer(3)

            dve.wait_ge(post_in, 16 * 9)
            for j in range(4):
                dve.wait_ge(pj_full, PJ_END + j + 1)
                dst = bc[:, j // 2, 512 * (j % 2):512 * (j % 2) + 512]
                dve.tensor_tensor(dst, pj[j % 2][:], dst, ALU.add).then_inc(pj_free[j % 2], 1)
            dve.wait_ge(ada2_c, 4)
            dve.tensor_tensor(ada_c[:, 2, :], sc_ps[1][:, 0:8], cols[:, 32:40], ALU.add)
            dve.scalar_tensor_tensor(out=ada_c[:, 3, :], in0=sc_ps[1][:, 8:16], scalar=1.0, in1=cols[:, 40:48],
                                     op0=ALU.add, op1=ALU.add).then_inc(ada2_r, 1)

            def layer_norm(t, turn):
                at = 2 * (ST * turn + t)
                for half in range(2):
                    dve.bn_stats(stats[:, t, half, :], tokens[:, t, 512 * half:512 * half + 512]).then_inc(ln_step, 1)
                dve.wait_ge(ln_step, at + 2)
                dve.bn_aggr(mv[:, t, :], stats[:, t].rearrange("p a b -> p (a b)")).then_inc(var_r, 1)
                dve.wait_ge(rstd_r, ST * turn + t + 1)
                dve.tensor_scalar(tokens[:, t, :], tokens[:, t, :], mv[:, t, 0:1], rstd[:, t:t + 1],
                                  ALU.subtract, ALU.mult).then_inc(norm_r, 1)

            dve.wait_ge(xres_in, 16)
            dve.wait_ge(pj_free[0], PJ_END // 2 + 2)
            dve.wait_ge(pj_free[1], PJ_END // 2 + 2)
            dve.wait_ge(mixed_r, KC * MIXERS)
            for n in range(2 * ST):
                half, t = divmod(n, ST)
                cut = slice(512 * half, 512 * half + 512)
                dve.wait_ge(pj_full, PJ_END + 5 + n)
                dve.tensor_tensor(gated[:, n % 2, :], pj[n % 2][:], bc[:, 0, cut], ALU.mult).then_inc(pj_free[n % 2], 1)
                dve.wait_ge(pj_free[n % 2], PJ_END // 2 + 3 + n // 2)
                dve.scalar_tensor_tensor(out=tokens[:, t, cut], in0=tokens[:, t, cut], scalar=ALPHA,
                                         in1=gated[:, n % 2, :], op0=ALU.mult, op1=ALU.add).then_inc(res_step, 1)
            for t in range(ST):
                dve.wait_ge(res_step, ST + t + 1)
                layer_norm(t, 0)

            step = [0]

            def link(ins):
                step[0] += 1
                ins.then_inc(rt, 1)
                dve.wait_ge(rt, step[0])

            score_r, biased, m_, v_, s1, s2, comb = (r[k][:] for k in ("score", "biased", "m", "v", "s1", "s2", "comb"))
            by_group = biased.rearrange("p t (g j) -> p (t g) j", g=GROUPS)
            gsum, gpair, gsel = (g4[k][:] for k in ("sum", "pair", "sel"))
            dve.wait_ge(sig_r, 1)
            for t in range(ST):
                ins = dve.tensor_tensor(biased[:, t, :], score_r[:, t, :], b_rb[:], ALU.add)
            link(ins)
            first = True
            for i in range(4):
                for j in range(i + 1, 4):
                    link(dve.tensor_tensor(gsum if first else gpair, by_group[:, :, i], by_group[:, :, j], ALU.add))
                    if not first:
                        link(dve.tensor_tensor(gsum, gsum, gpair, ALU.max))
                    first = False

            def first_best(dst, src, n, peak_t, tmp, ranks):
                for t in range(ST):
                    ins = dve.tensor_reduce(peak_t[:, t:t + 1], src[:, t, :], AX_X, ALU.max)
                link(ins)
                for t in range(ST):
                    ins = dve.scalar_tensor_tensor(out=tmp[:, t, :], in0=src[:, t, :], scalar=peak_t[:, t:t + 1],
                                                   in1=ranks, op0=ALU.is_equal, op1=ALU.mult)
                link(ins)
                for t in range(ST):
                    ins = dve.tensor_reduce(peak_t[:, t:t + 1], tmp[:, t, :], AX_X, ALU.max)
                link(ins)
                for t in range(ST):
                    ins = dve.tensor_scalar(dst[:, t, :], tmp[:, t, :], peak_t[:, t:t + 1], None, ALU.is_equal)
                link(ins)

            tg = lambda v: v.rearrange("p (t g) -> p t g", t=ST)
            first_best(tg(gsel), tg(gsum), GROUPS, one["a"][:], tg(gpair), rank[:, 0:GROUPS])
            link(dve.tensor_scalar(gsel, gsel, 1.0, -MASKED, ALU.subtract, ALU.mult))
            m_g = m_.rearrange("p t (g j) -> p (t g) j", g=GROUPS)
            for j in range(4):
                ins = dve.tensor_tensor(m_g[:, :, j], by_group[:, :, j], gsel, ALU.add)
            link(ins)
            first_best(s1, m_, E, one["a"][:], v_, rank[:, GROUPS:GROUPS + E])
            link(dve.scalar_tensor_tensor(out=m_, in0=s1, scalar=10 * MASKED, in1=m_, op0=ALU.mult, op1=ALU.add))
            first_best(s2, m_, E, one["a"][:], v_, rank[:, GROUPS:GROUPS + E])
            link(dve.tensor_tensor(s1, s1, s2, ALU.add))
            link(dve.tensor_tensor(v_, s1, score_r, ALU.mult))
            link(dve.tensor_reduce(one["a"][:], v_, AX_X, ALU.add))
            link(dve.reciprocal(one["b"][:], one["a"][:]))
            for t in range(ST):
                ins = dve.tensor_scalar(comb[:, t, :], v_[:, t, :], one["b"][:, t:t + 1], None, ALU.mult)
            link(ins)

            dve.wait_ge(acc_zero, 1)
            with dve.Fori(0, E) as e:
                for f in range(FC):
                    dve.wait_ge(silu_r, FC * e + f + 1)
                    dve.tensor_tensor(hidT[:, f, :], banks[2 * (f % 2) + 1][:], silu_t[:, f % 2, :], ALU.mult)\
                       .then_inc(hid_r, 1)
                for n in range(2 * ST):
                    half, t = divmod(n, ST)
                    cut = slice(512 * half, 512 * half + 512)
                    dve.wait_ge(down_full, 8 * e + n + 1)
                    dve.scalar_tensor_tensor(out=acc[:, t, cut], in0=banks[4 + n % 4][:],
                                             scalar=comb[:, t, bass.ds(e, 1)], in1=acc[:, t, cut],
                                             op0=ALU.mult, op1=ALU.add).then_inc(acc_r, 1)
                dve.wait_ge(acc_r, 8 * e + 8)

            for t in range(ST):
                dve.tensor_tensor(acc[:, t, :], acc[:, t, :], bc[:, 1, :], ALU.mult).then_inc(res_step, 1)
                dve.wait_ge(res_step, 2 * ST + 2 * t + 1)
                dve.scalar_tensor_tensor(out=tokens[:, t, :], in0=tokens[:, t, :], scalar=ALPHA,
                                         in1=acc[:, t, :], op0=ALU.mult, op1=ALU.add).then_inc(res_step, 1)
                dve.wait_ge(res_step, 2 * ST + 2 * t + 2)
                layer_norm(t, 1)

        @block.gpsimd
        def _(pool):
            pool.wait_ge(pj_full, 4)
            pool.memset(mixedT[:], 0.0).then_inc(mixed_zero, 1)
            pool.memset(minus_half[:], -0.5).then_inc(half_r, 1)
            pool.wait_ge(mixed_zero, 1)
            pool.wait_ge(half_r, 1)
            pool.wait_ge(masks_in, 16)

            def mixer(n, indexer):
                half = PJ0 // 2 + PJN // 2 * n
                for j in range(HPM):
                    pool.wait_ge(row_in[j % 2], 16 * (2 * n + j // 2 + 1))
                    if j >= 2:
                        pool.wait_ge(logits_r, STEPS * n + ST * (j - 1))
                    if not indexer:
                        pool.tensor_tensor(pool_waits[:, j:j + 1], minus_half[:], minus_half[:], ALU.add)
                        pool.tensor_tensor(bias_t[:, j % 2, :], row_b[:, j % 2, :],
                                           mask_t[:, bass.ds(n, 1), :].rearrange("p o n -> p (o n)"), ALU.add)\
                            .then_inc(bias_r, 1)
                        continue
                    if j == 0:
                        pool.wait_ge(topk_done, ST - 1)
                    pool.tensor_tensor(bias_t[:, j % 2, 0:P], row_b[:, j % 2, 0:P], mask_t[:, 1, 0:P], ALU.add)
                    for i in range(1, ST):
                        ins = pool.tensor_tensor(bias_t[:, j % 2, OFF[i]:OFF[i + 1]], row_b[:, j % 2, OFF[i]:OFF[i + 1]],
                                                 score[:, i - 1, 0:P * i + P], ALU.add)
                    ins.then_inc(bias_r, 1)
                for c in range(KC):
                    pool.wait_ge(pj_free[c % 2], half + 9 + c // 2)
                    pool.tensor_tensor(mixedT[:, c, :], mixedT[:, c, :], gated[:, c % 2, :], ALU.add).then_inc(mixed_r, 1)
                pool.wait_ge(mixed_r, KC * n + KC)

            with pool.Fori(0, 3) as n:
                mixer(n, False)
            mixer(3, True)

            def root(t, turn):
                pool.wait_ge(var_r, ST * turn + t + 1)
                pool.tensor_scalar(rstd[:, t:t + 1], mv[:, t, 1:2], EPS, None, ALU.add).then_inc(eps_r, 1)
                pool.wait_ge(eps_r, ST * turn + t + 1)
                pool.tensor_tensor(rstd[:, t:t + 1], rstd[:, t:t + 1], minus_half[:], ALU.pow).then_inc(rstd_r, 1)

            def gain(t, turn, done):
                pool.wait_ge(norm_r, ST * turn + t + 1)
                pool.tensor_tensor(tokens[:, t, :], tokens[:, t, :], bc[:, 2 + 2 * turn, :], ALU.mult).then_inc(gain_r, 1)
                pool.wait_ge(gain_r, ST * turn + t + 1)
                pool.tensor_tensor(tokens[:, t, :], tokens[:, t, :], bc[:, 3 + 2 * turn, :], ALU.add).then_inc(done, 1)

            for t in range(ST + 1):
                if t < ST:
                    root(t, 0)
                if t:
                    gain(t - 1, 0, x1_r)
            pool.wait_ge(pj_full, PJ_END + 12)
            pool.memset(acc, 0.0).then_inc(acc_zero, 1)
            for t in range(ST + 1):
                if t < ST:
                    root(t, 1)
                if t:
                    gain(t - 1, 1, fin_r)


INPUTS = ["x", "c", "w_in", "b_forget", "w_branch", "w_merge_gate", "w_out", "w_ada", "b_ada", "ln1_g", "ln1_b",
          "ln2_g", "ln2_b", "w_router", "b_router", "w_exp_gate", "w_exp_up", "w_exp_down"]


def kernel(**inputs):
    import concourse.bacc as bacc
    from concourse.bass_utils import run_bass_kernel_spmd

    nc = bacc.Bacc("TRN2", target_bir_lowering=False, num_devices=1)
    arrays = {name: np.ascontiguousarray(inputs[name]) for name in INPUTS}
    arrays.update(constants())
    aps = {name: nc.dram_tensor("in_" + name, v.shape, F32, kind="ExternalInput").ap() for name, v in arrays.items()}
    out = nc.dram_tensor("out_x", (1, S, D), F32, kind="ExternalOutput").ap()
    build(nc, aps, out)
    result = run_bass_kernel_spmd(nc, [{"in_" + name: v for name, v in arrays.items()}], core_ids=[0])
    return result.results[0]["out_x"]
```
